# Optimizing a Trainium2 kernel written in Bass

```python
import math
import jax, jax.numpy as jnp
from jax import lax
import numpy as np

D_MODEL = 2048
BATCH = 1
SEQ = 256
DEPTH = 1

HEAD_DIM = 128
A_Q_HEADS = 8
A_KV_HEADS = 2
A_WINDOW = 128
A_BLOCK = 128
B_HEADS = 8
GRID_W = 64
B_WIN_R = 8
B_WIN_C = 16
B_QBLK_R = 8
B_QBLK_C = 16
D_FF = 5632
MACARON_W = 0.5
RMS_EPS = 1e-6
NEG_INF = -1e30

A_Q_W = A_Q_HEADS * HEAD_DIM
A_KV_W = A_KV_HEADS * HEAD_DIM
B_W = B_HEADS * HEAD_DIM
IN_PROJ_W = A_Q_W + 2 * A_KV_W + 3 * B_W + 2 * D_MODEL

kernel_name = "hybrid_window_gqa_natten2d_macaron"

def rms_norm(x, g):
    xf = x.astype(jnp.float32)
    y = xf * lax.rsqrt(jnp.mean(xf * xf, axis=-1, keepdims=True) + RMS_EPS)
    return (y * g.astype(jnp.float32)).astype(x.dtype)

def swiglu_ffn(x, w_in, w_out):
    g, u = jnp.split(x @ w_in, 2, axis=-1)
    return (jax.nn.silu(g) * u) @ w_out

def alibi_slopes(n_heads):
    return np.array([2.0 ** (-8.0 * (i + 1) / n_heads) for i in range(n_heads)], dtype=np.float32)

def windowed_gqa(q, k, v, sink):
    b, s, hq, d = q.shape
    hkv = k.shape[2]
    grp = hq // hkv
    nb = s // A_BLOCK
    nshift = 1 + 2 * (A_WINDOW // A_BLOCK)
    span = nshift * A_BLOCK
    pad = ((0, 0), (A_WINDOW, A_WINDOW), (0, 0), (0, 0))
    kp = jnp.pad(k, pad)
    vp = jnp.pad(v, pad)
    kb = jnp.concatenate([kp[:, j * A_BLOCK: j * A_BLOCK + s].reshape(b, nb, A_BLOCK, hkv, d)
                          for j in range(nshift)], axis=2)
    vb = jnp.concatenate([vp[:, j * A_BLOCK: j * A_BLOCK + s].reshape(b, nb, A_BLOCK, hkv, d)
                          for j in range(nshift)], axis=2)
    qb = q.reshape(b, nb, A_BLOCK, hkv, grp, d)
    scores = jnp.einsum('bnqkgd,bnskd->bnkgqs', qb, kb).astype(jnp.float32) * (d ** -0.5)
    a = np.arange(A_BLOCK)[:, None]
    jj = np.arange(span)[None, :]
    absd = np.abs(a + A_WINDOW - jj).astype(np.float32)
    key_pos = np.arange(nb)[:, None, None] * A_BLOCK - A_WINDOW + jj[None]
    valid = (absd[None] <= A_WINDOW) & (key_pos >= 0) & (key_pos < s)
    slopes = alibi_slopes(hq).reshape(hkv, grp, 1, 1)
    bias = jnp.asarray(-slopes * absd[None, None])
    logits = jnp.where(jnp.asarray(valid)[None, :, None, None], scores + bias[None, None], NEG_INF)
    sink_l = jnp.broadcast_to(sink.astype(jnp.float32).reshape(1, 1, hkv, grp, 1, 1),
                              logits.shape[:-1] + (1,))
    p = jax.nn.softmax(jnp.concatenate([logits, sink_l], axis=-1), axis=-1)[..., :-1]
    out = jnp.einsum('bnkgqs,bnskd->bnqkgd', p.astype(v.dtype), vb)
    return out.reshape(b, s, hq * d)

def neighbourhood_attention_2d(q, k, v, rpb):
    b, s, h, d = q.shape
    rows = s // GRID_W
    kr = min(B_WIN_R, rows)
    kc = min(B_WIN_C, GRID_W)
    qr = math.gcd(rows, B_QBLK_R)
    qc = math.gcd(GRID_W, B_QBLK_C)
    lr = min(qr + kr - 1, rows)
    lc = min(qc + kc - 1, GRID_W)
    nrb = rows // qr
    ncb = GRID_W // qc
    rs = np.clip(np.arange(rows) - kr // 2, 0, rows - kr)
    cs = np.clip(np.arange(GRID_W) - kc // 2, 0, GRID_W - kc)
    key_rows = np.minimum(rs[::qr], rows - lr)[:, None] + np.arange(lr)
    key_cols = np.minimum(cs[::qc], GRID_W - lc)[:, None] + np.arange(lc)
    q_rows = np.arange(nrb)[:, None] * qr + np.arange(qr)
    q_cols = np.arange(ncb)[:, None] * qc + np.arange(qc)
    dr = key_rows[:, None, :] - q_rows[:, :, None]
    dc = key_cols[:, None, :] - q_cols[:, :, None]
    rstart = rs[q_rows][:, :, None]
    cstart = cs[q_cols][:, :, None]
    vr = (key_rows[:, None, :] >= rstart) & (key_rows[:, None, :] < rstart + kr)
    vc = (key_cols[:, None, :] >= cstart) & (key_cols[:, None, :] < cstart + kc)
    full = (nrb, ncb, qr, qc, lr, lc)
    valid = (vr[:, None, :, None, :, None] & vc[None, :, None, :, None, :]).reshape(nrb, ncb, qr * qc, lr * lc)
    ridx = np.broadcast_to(np.clip(dr + B_WIN_R - 1, 0, 2 * B_WIN_R - 2)[:, None, :, None, :, None], full)
    cidx = np.broadcast_to(np.clip(dc + B_WIN_C - 1, 0, 2 * B_WIN_C - 2)[None, :, None, :, None, :], full)
    ridx = ridx.reshape(nrb, ncb, qr * qc, lr * lc)
    cidx = cidx.reshape(nrb, ncb, qr * qc, lr * lc)
    bias = rpb.astype(jnp.float32)[:, ridx, cidx].transpose(1, 2, 0, 3, 4)

    def gather_blocks(t):
        t5 = t.reshape(b, rows, GRID_W, h, d)
        tr = jnp.take(t5, key_rows.reshape(-1), axis=1).reshape(b, nrb, lr, GRID_W, h, d)
        tb = jnp.take(tr, key_cols.reshape(-1), axis=3).reshape(b, nrb, lr, ncb, lc, h, d)
        return tb.transpose(0, 1, 3, 2, 4, 5, 6).reshape(b, nrb, ncb, lr * lc, h, d)

    qg = q.reshape(b, nrb, qr, ncb, qc, h, d).transpose(0, 1, 3, 2, 4, 5, 6).reshape(b, nrb, ncb, qr * qc, h, d)
    kg = gather_blocks(k)
    vg = gather_blocks(v)
    scores = jnp.einsum('bijqhd,bijkhd->bijhqk', qg, kg).astype(jnp.float32) * (d ** -0.5)
    logits = jnp.where(jnp.asarray(valid)[None, :, :, None], scores + bias[None], NEG_INF)
    p = jax.nn.softmax(logits, axis=-1)
    out = jnp.einsum('bijhqk,bijkhd->bijqhd', p.astype(v.dtype), vg)
    out = out.reshape(b, nrb, ncb, qr, qc, h * d).transpose(0, 1, 3, 2, 4, 5)
    return out.reshape(b, s, h * d)

def hybrid_mixer(u, w_in, b_gate, sink_a, rpb_b, w_up_a, w_up_b, w_out):
    b, s, _ = u.shape
    cuts = np.cumsum([A_Q_W, A_KV_W, A_KV_W, B_W, B_W, B_W, D_MODEL]).tolist()
    qa, ka, va, qb, kb, vb, ga, gb = jnp.split(u @ w_in, cuts, axis=-1)
    bga, bgb = jnp.split(b_gate, 2)
    ya = windowed_gqa(qa.reshape(b, s, A_Q_HEADS, HEAD_DIM),
                      ka.reshape(b, s, A_KV_HEADS, HEAD_DIM),
                      va.reshape(b, s, A_KV_HEADS, HEAD_DIM), sink_a) @ w_up_a
    yb = neighbourhood_attention_2d(qb.reshape(b, s, B_HEADS, HEAD_DIM),
                                    kb.reshape(b, s, B_HEADS, HEAD_DIM),
                                    vb.reshape(b, s, B_HEADS, HEAD_DIM), rpb_b) @ w_up_b
    m = jax.nn.sigmoid(ga + bga) * ya + jax.nn.sigmoid(gb + bgb) * yb
    return m @ w_out

def setup_inputs(seed: int = 0) -> dict:
    key = jax.random.key(seed)
    ks = jax.random.split(key, 20)
    f32 = jnp.float32

    def w(k, shape, fan_in):
        return jax.random.normal(k, shape, f32) * (fan_in ** -0.5)

    def gain(k):
        return 1.0 + 0.05 * jax.random.normal(k, (DEPTH, D_MODEL), f32)

    return {
        "x": jax.random.normal(ks[0], (BATCH, SEQ, D_MODEL), f32),
        "ffn1_pre_g": gain(ks[1]),
        "ffn1_w_in": w(ks[2], (DEPTH, D_MODEL, 2 * D_FF), D_MODEL),
        "ffn1_w_out": w(ks[3], (DEPTH, D_FF, D_MODEL), D_FF),
        "ffn1_post_g": gain(ks[4]),
        "mix_pre_g": gain(ks[5]),
        "w_in": w(ks[6], (DEPTH, D_MODEL, IN_PROJ_W), D_MODEL),
        "b_gate": 0.01 * jax.random.normal(ks[7], (DEPTH, 2 * D_MODEL), f32),
        "sink_a": jax.random.normal(ks[8], (DEPTH, A_Q_HEADS), f32),
        "rpb_b": 0.02 * jax.random.normal(ks[9], (DEPTH, B_HEADS, 2 * B_WIN_R - 1, 2 * B_WIN_C - 1), f32),
        "w_up_a": w(ks[10], (DEPTH, A_Q_W, D_MODEL), A_Q_W),
        "w_up_b": w(ks[11], (DEPTH, B_W, D_MODEL), B_W),
        "w_out": w(ks[12], (DEPTH, D_MODEL, D_MODEL), D_MODEL),
        "mix_post_g": gain(ks[13]),
        "ffn2_pre_g": gain(ks[14]),
        "ffn2_w_in": w(ks[15], (DEPTH, D_MODEL, 2 * D_FF), D_MODEL),
        "ffn2_w_out": w(ks[16], (DEPTH, D_FF, D_MODEL), D_FF),
        "ffn2_post_g": gain(ks[17]),
    }

def reference(x, ffn1_pre_g, ffn1_w_in, ffn1_w_out, ffn1_post_g, mix_pre_g, w_in, b_gate, sink_a,
              rpb_b, w_up_a, w_up_b, w_out, mix_post_g, ffn2_pre_g, ffn2_w_in, ffn2_w_out, ffn2_post_g):
    h = x
    for l in range(DEPTH):
        f1 = swiglu_ffn(rms_norm(h, ffn1_pre_g[l]), ffn1_w_in[l], ffn1_w_out[l])
        h = h + MACARON_W * rms_norm(f1, ffn1_post_g[l])
        mix = hybrid_mixer(rms_norm(h, mix_pre_g[l]), w_in[l], b_gate[l], sink_a[l], rpb_b[l],
                           w_up_a[l], w_up_b[l], w_out[l])
        h = h + rms_norm(mix, mix_post_g[l])
        f2 = swiglu_ffn(rms_norm(h, ffn2_pre_g[l]), ffn2_w_in[l], ffn2_w_out[l])
        h = h + MACARON_W * rms_norm(f2, ffn2_post_g[l])
    return h


_drawn_inputs = setup_inputs


def setup_inputs(seed=0):
    import zlib

    import numpy as np

    out = dict(_drawn_inputs(seed))
    spreads = {}
    factors = {'b_gate': 8.0, 'rpb_b': 6.602, 'ffn2_post_g': 3.582}
    for name, (base, spread) in spreads.items():
        noise = np.random.default_rng([zlib.crc32(name.encode()), seed]).standard_normal(out[name].shape)
        drawn = base * np.exp(spread * noise) if base else spread * noise
        out[name] = __import__('jax').numpy.asarray(drawn.astype(out[name].dtype))
    for name, factor in factors.items():
        out[name] = (out[name] * factor).astype(out[name].dtype)
    return out
```

```python
import concourse.bass as bass
from concourse import mybir
import numpy as np

F32 = mybir.dt.float32
F32R = mybir.dt.float32r
ALU = mybir.AluOpType
ACT = mybir.ActivationFunctionType
AX = mybir.AxisListType

P = 128
SEQ = 256
TT = SEQ // P
D = 2048
DC = D // P
DFF = 5632
FC = DFF // P
NB = 512
QK_BLOCKS = 9
GATE_BLOCKS = 2 * D // NB
A_Q, A_KV, B_H = 8, 2, 8
HD = 128
SCALE = HD ** -0.5
GRID_W, ROWS = 64, SEQ // 64
RPB_C = 31
RPB_USED = 2 * ROWS - 1
PADW = 2 * GRID_W - 1
EPS = 1e-6

RAW = 4
WS = 8
AHEAD = WS - 1

FFN_IN_BLOCKS = 2 * DFF // NB
OUT_BLOCKS = D // NB
C_F1IN = 0
C_F1OUT = C_F1IN + FFN_IN_BLOCKS * DC
C_QKV = C_F1OUT + OUT_BLOCKS * FC
C_GATE = C_QKV + QK_BLOCKS * DC
C_UP = C_GATE + GATE_BLOCKS * DC
C_WOUT = C_UP + OUT_BLOCKS * 2 * A_Q
C_F2IN = C_WOUT + OUT_BLOCKS * DC
C_F2OUT = C_F2IN + FFN_IN_BLOCKS * DC
C_END = C_F2OUT + OUT_BLOCKS * FC

B_F1IN = 0
B_F1OUT = B_F1IN + FFN_IN_BLOCKS
B_QKV = B_F1OUT + OUT_BLOCKS
B_GATE = B_QKV + QK_BLOCKS
B_UP = B_GATE + GATE_BLOCKS
B_WOUT = B_UP + 2 * OUT_BLOCKS
B_F2IN = B_WOUT + OUT_BLOCKS
B_F2OUT = B_F2IN + FFN_IN_BLOCKS
B_END = B_F2OUT + OUT_BLOCKS

M_F1 = 0
M_MIX = FFN_IN_BLOCKS // 2
M_F2 = M_MIX + OUT_BLOCKS

QK_HEADS = [(0, 4), (4, 4), (8, 2), (10, 4), (14, 4), (18, 4), (22, 4)]
SLOPES = [2.0 ** (-8.0 * (i + 1) / A_Q) for i in range(A_Q)]


def freed_before(b):
    return b // 2 * TT


def chunks_through(b):
    for first_b, first_c, chunks in ((B_F2OUT, C_F2OUT, FC), (B_F2IN, C_F2IN, DC), (B_WOUT, C_WOUT, DC), (B_UP, C_UP, 8),
                                     (B_QKV, C_QKV, DC), (B_F1OUT, C_F1OUT, FC), (B_F1IN, C_F1IN, DC)):
        if b >= first_b:
            return first_c + (b - first_b + 1) * chunks


def layer_kernel(nc, x, ffn1_pre_g, ffn1_w_in, ffn1_w_out, ffn1_post_g, mix_pre_g, w_in, b_gate,
                 sink_a, rpb_b, w_up_a, w_up_b, w_out, mix_post_g, ffn2_pre_g, ffn2_w_in,
                 ffn2_w_out, ffn2_post_g, alibi_dist, natten_mask, out):
    from contextlib import ExitStack
    ctx = ExitStack()
    with ctx:
        at = [((nc.sbuf_base + 31) // 32) * 32]

        def place(name, shape, dt, offset=None):
            size = int(np.prod(shape[1:])) * 4
            if offset is None:
                size = -(-size // 32) * 32
                offset = at[0]
                at[0] += size
            return nc.alloc_sbuf_tensor_at(name, shape, dt, offset=offset), offset

        h, _ = place("h", [P, TT, D], F32)
        XH, _ = place("XH", [P, DC, SEQ], F32R)
        XL, o_xl = place("XL", [P, DC, SEQ], F32R)
        MH, o_m = place("MH", [P, FC, SEQ], F32R)
        ML, _ = place("ML", [P, FC, SEQ], F32R)
        raw, _ = place("raw", [P, RAW, 2, NB], F32)
        WH, _ = place("WH", [P, WS, NB], F32R)
        WL, _ = place("WL", [P, WS, NB], F32R)
        tmp, o_tmp = place("tmp", [P, TT, NB], F32)
        YL, o_yl = place("YL", [P, 8, 2, SEQ], F32R)
        ident, _ = place("ident", [P, P], F32)
        gainT, _ = place("gainT", [P, 3 * DC], F32)
        sink, _ = place("sink", [P, A_Q], F32)
        ssq, _ = place("ssq", [P, 6, TT, OUT_BLOCKS], F32)
        ms, _ = place("ms", [P, 6, TT], F32)
        rstd, _ = place("rstd", [P, 6, TT], F32)
        neghalf, _ = place("neghalf", [P, TT], F32)
        smax, _ = place("smax", [P, 16, TT], F32)
        nmax, _ = place("nmax", [P, 16, TT], F32)
        psum_, _ = place("psum_", [P, 16, TT], F32)
        esink, _ = place("esink", [P, 16, TT], F32)
        rinv, _ = place("rinv", [P, 16, TT], F32)
        fg, _ = place("fg", [P, TT, D], F32, o_yl)
        gp_ffn, _ = place("gp_ffn", [P, D], F32, o_xl)
        o = o_m
        QT, _ = place("QT", [P, 26, SEQ], F32, o); o += 26 * SEQ * 4
        V, _ = place("V", [P, TT, 10 * HD], F32, o); o += TT * 10 * HD * 4
        o_gates = o
        gates, _ = place("gates", [P, TT, 2 * D], F32, o); o += TT * 2 * D * 4
        biasB, _ = place("biasB", [P, B_H, TT, SEQ], F32, o)
        YH, _ = place("YH", [P, 8, 2, SEQ], F32R, o); o += 8 * 2 * SEQ * 4
        distA, _ = place("distA", [P, TT, SEQ], F32, o); o += TT * SEQ * 4
        o_mask = o
        maskB, _ = place("maskB", [P, TT, SEQ], F32, o); o += TT * SEQ * 4
        assert o == o_m + 2 * FC * SEQ * 4
        gp_mix, _ = place("gp_mix", [P, D], F32, o_gates)
        prob = [place("prob_b", [P, TT, SEQ], F32, o_tmp)[0],
                place("prob_a", [P, TT, SEQ], F32, o_mask)[0]]
        probT, _ = place("probT", [P, TT, SEQ], F32, o_tmp + TT * SEQ * 4)
        rpad, _ = place("rpad", [B_H * RPB_USED, PADW], F32, o_yl)
        grows, _ = place("grows", [3 * DC, P], F32, o_yl + 1024)
        rscr = nc.dram_tensor("rpb_padded", [B_H * RPB_USED * GRID_W * PADW], F32)

        acc = ctx.enter_context(nc.psum_tensor("acc", [P, 4, NB], F32))
        tp = ctx.enter_context(nc.psum_tensor("tp", [P, 4, NB], F32))

        def sem(name):
            return ctx.enter_context(nc.semaphore(name))

        x_landed = [sem(f"x_landed{i}") for i in range(OUT_BLOCKS)]
        raw_landed = [sem(f"raw_landed{i}") for i in range(RAW)]
        gain_landed, sink_landed, post_gain_landed, gate_bias_landed, masks_landed, rpb_landed = map(
            sem, ["gain_landed", "sink_landed", "post_gain_landed", "gate_bias_landed", "masks_landed", "rpb_landed"])
        ident_ready, consts_ready, gain_ready, bias_ready = map(
            sem, ["ident_ready", "consts_ready", "gain_ready", "bias_ready"])
        pad_zeroed, pad_landed, pad_stored = map(sem, ["pad_zeroed", "pad_landed", "pad_stored"])
        hi_ready, lo_ready, chunk_done = sem("hi_ready"), sem("lo_ready"), sem("chunk_done")
        acc_freed = [sem("acc_freed0"), sem("acc_freed1")]
        h_ready, xt_turned, xt_hi, xt_lo = map(sem, ["h_ready", "xt_turned", "xt_hi", "xt_lo"])
        squares_ready, ms_ready, rstd_ready = map(sem, ["squares_ready", "ms_ready", "rstd_ready"])
        m_ready, mt_turned, mt_hi, mt_lo = map(sem, ["m_ready", "mt_turned", "mt_hi", "mt_lo"])
        qt_turned, qt_act, qt_dve = map(sem, ["qt_turned", "qt_act", "qt_dve"])
        scores_done, logits_ready, nmax_ready, exp_ready, prob_ready = map(
            sem, ["scores_done", "logits_ready", "nmax_ready", "exp_ready", "prob_ready"])
        prob_turned, probT_ready, y_done, y_hi, y_lo = map(
            sem, ["prob_turned", "probT_ready", "y_done", "y_hi", "y_lo"])
        sig_ready = sem("sig_ready")
        dve_step = sem("dve_step")
        stored = sem("stored")

        W1I, W1O, WIN, WOUT = ffn1_w_in[0], ffn1_w_out[0], w_in[0], w_out[0]
        W2I, W2O, UPA, UPB = ffn2_w_in[0], ffn2_w_out[0], w_up_a[0], w_up_b[0]
        x_tiles = x.rearrange("b (t p) d -> p (b t) d", p=P)
        out_tiles = out.rearrange("b (t p) d -> p (b t) d", p=P)

        block = ctx.enter_context(nc.Block())

        @block.sync
        def _(sp):
            def load(chunk, weights, chunks, col, more=0):
                for k in range(0, chunks, 2):
                    piece = (chunk + k) // 2
                    if piece >= RAW:
                        sp.wait_ge(lo_ready, 2 * (piece - RAW) + 2 + more)
                    src = weights[k * P:(k + 2) * P, bass.ds(col, NB)].rearrange("(c p) n -> p c n", p=P)
                    sp.dma_start(raw[:, piece % RAW, :, :], src).then_inc(raw_landed[piece % RAW], 16)

            def ffn(c_in, c_out, wi, wo, first=0):
                load(c_in + first, wi[first * P:, :], DC - first, 0)
                with sp.Fori(0, DFF // NB - 1) as i:
                    load(c_in + DC, wi, DC, i * NB + DFF, i * (2 * DC))
                    load(c_in + 2 * DC, wi, DC, i * NB + NB, i * (2 * DC))
                load(c_out - DC, wi, DC, 2 * DFF - NB)
                for b in range(OUT_BLOCKS):
                    load(c_out + b * FC, wo, FC, b * NB)

            for j in range(OUT_BLOCKS):
                sp.dma_start(h[:, :, j * NB:(j + 1) * NB], x_tiles[:, :, j * NB:(j + 1) * NB]).then_inc(x_landed[j], 16)
                if j == 0:
                    for n, g in enumerate((ffn1_pre_g, mix_pre_g, ffn2_pre_g)):
                        sp.dma_start(grows[n * DC:(n + 1) * DC, :],
                                     g[0].rearrange("(c p) -> c p", p=P)).then_inc(gain_landed, 16)
                load(C_F1IN + 2 * j, W1I[2 * j * P:, :], 2, 0)
            ffn(C_F1IN, C_F1OUT, W1I, W1O, 2 * OUT_BLOCKS)
            for b in range(QK_BLOCKS + GATE_BLOCKS):
                load(C_QKV + b * DC, WIN, DC, b * NB)
            for u in range(OUT_BLOCKS):
                load(C_UP + u * 16, UPA, 8, u * NB)
                load(C_UP + u * 16 + 8, UPB, 8, u * NB)
            for b in range(OUT_BLOCKS):
                load(C_WOUT + b * DC, WOUT, DC, b * NB)
            ffn(C_F2IN, C_F2OUT, W2I, W2O)
            for j in range(OUT_BLOCKS):
                for t in range(TT):
                    sp.wait_ge(h_ready, 2 * TT * OUT_BLOCKS + TT * j + t + 1)
                    sp.dma_start(out_tiles[:, t, j * NB:(j + 1) * NB], h[:, t, j * NB:(j + 1) * NB]).then_inc(stored, 16)
            sp.wait_ge(stored, 16 * TT * OUT_BLOCKS)

        @block.gpsimd
        def _(pool):
            pool.memset(ident[:, :], 0.0).then_inc(ident_ready, 1)
            pool.wait_ge(ident_ready, 1)
            pool.affine_select(out=ident[:, :], in_=ident[:, :], compare_op=ALU.not_equal, fill=1.0, base=0,
                               pattern=[[-1, P]], channel_multiplier=1).then_inc(ident_ready, 1)
            pool.dma_start(sink[:, :], sink_a.broadcast_to([P, A_Q])).then_inc(sink_landed, 16)

            def inverse_root(n):
                pool.wait_ge(consts_ready, 1)
                pool.wait_ge(ms_ready, n + 1)
                pool.tensor_tensor(rstd[:, n, :], ms[:, n, :], neghalf[:, :], ALU.pow).then_inc(rstd_ready, 1)

            inverse_root(0)
            pool.memset(rpad[:, :], 0.0).then_inc(pad_zeroed, 1)
            pool.wait_ge(pad_zeroed, 1)
            for hd in range(B_H):
                pool.dma_start(rpad[hd * RPB_USED:(hd + 1) * RPB_USED, GRID_W - 16:GRID_W - 16 + RPB_C],
                               rpb_b[0, hd, 8 - ROWS:7 + ROWS, :]).then_inc(pad_landed, 16)
            pool.wait_ge(pad_landed, 16 * B_H)
            for hd in range(B_H):
                rows = slice(hd * RPB_USED, (hd + 1) * RPB_USED)
                pool.dma_start(rscr[:].rearrange("(a c b) -> a c b", c=GRID_W, b=PADW)[rows],
                               rpad[rows, :].unsqueeze(1).broadcast_to([RPB_USED, GRID_W, PADW])).then_inc(pad_stored, 16)
            pool.wait_ge(pad_stored, 16 * B_H)
            pool.wait_ge(chunk_done, C_F1OUT)
            pool.dma_start(gp_ffn[:, :], ffn1_post_g.broadcast_to([P, D])).then_inc(post_gain_landed, 16)
            pool.wait_ge(chunk_done, C_QKV)
            pool.dma_start(distA[:, :, :], alibi_dist.rearrange("(t p) k -> p t k", p=P)).then_inc(masks_landed, 16)
            pool.dma_start(maskB[:, :, :], natten_mask.rearrange("(t p) k -> p t k", p=P)).then_inc(masks_landed, 16)
            inverse_root(1)
            inverse_root(2)
            for b in range(GATE_BLOCKS):
                pool.wait_ge(chunk_done, C_QKV + b * DC)
                if b:
                    pool.wait_ge(gate_bias_landed, 16 * TT * b)
                cols = slice(b * NB, (b + 1) * NB)
                for t in range(TT):
                    pool.dma_start(gates[:, t, cols], b_gate[:, cols].broadcast_to([P, NB])).then_inc(gate_bias_landed, 16)
                if b < ROWS:
                    r = b
                    half = slice((r % 2) * GRID_W, (r % 2 + 1) * GRID_W)
                    for hd in range(B_H):
                        first = (hd * RPB_USED + ROWS - 1 - r) * GRID_W * PADW + GRID_W - 1
                        src = bass.AP(rscr, first, [[PADW - 1, GRID_W], [GRID_W * PADW, ROWS], [1, GRID_W]])
                        dst = biasB[half, hd, r // 2, :].rearrange("p (a b) -> p a b", a=ROWS)
                        pool.dma_start(dst, src).then_inc(rpb_landed, 16)
            pool.wait_ge(masks_landed, 32)
            pool.wait_ge(rpb_landed, 16 * ROWS * B_H)
            for hd in range(B_H):
                pool.tensor_tensor(biasB[:, hd, :, :], biasB[:, hd, :, :], maskB[:, :, :], ALU.add).then_inc(bias_ready, 1)
            pool.wait_ge(m_ready, TT * OUT_BLOCKS)
            pool.dma_start(gp_mix[:, :], mix_post_g.broadcast_to([P, D])).then_inc(post_gain_landed, 16)
            inverse_root(3)
            inverse_root(4)
            pool.wait_ge(chunk_done, C_F2OUT)
            pool.dma_start(gp_ffn[:, :], ffn2_post_g.broadcast_to([P, D])).then_inc(post_gain_landed, 16)
            inverse_root(5)

        @block.scalar
        def _(act):
            def split_hi(c, more=0):
                if c % 2 == 0:
                    act.wait_ge(raw_landed[c // 2 % RAW], 16 * (c // 2 // RAW + 1) + more * (16 // (2 * RAW)))
                if c >= WS:
                    act.wait_ge(chunk_done, c - WS + 1 + more)
                act.activation(WH[:, c % WS, :], raw[:, c // 2 % RAW, c % 2, :], ACT.Copy).then_inc(hi_ready, 1)

            def normed_hi(n, c):
                act.wait_ge(xt_turned, DC * n + c + 1)
                act.activation(XH[:, c, :], tp[:, c % 4, 0:SEQ], ACT.Copy,
                               scale=gainT[:, n * DC + c:n * DC + c + 1]).then_inc(xt_hi, 1)

            def squares_before(norm, j, t):
                count = TT * OUT_BLOCKS * norm + TT * j + t
                if count >= TT:
                    act.wait_ge(squares_ready, count - TT + 1)

            def h_square(n, j, t):
                if n:
                    act.wait_ge(h_ready, TT * OUT_BLOCKS * (n - 1) + TT * (j + 1))
                else:
                    act.wait_ge(x_landed[j], 16)
                squares_before(2 * n, j, t)
                act.activation(tmp[:, t, :], h[:, t, j * NB:(j + 1) * NB], ACT.Square,
                               accum_out=ssq[:, 2 * n, t, j:j + 1]).then_inc(squares_ready, 1)

            def silu_gate(b, j, norm, di=0):
                act.wait_ge(chunk_done, chunks_through(b) + 2 * DC * di)
                act.wait_ge(rstd_ready, norm + 1)
                act.wait_ge(mt_turned, j + 1 + di)
                for t in range(TT):
                    act.activation(tmp[:, t, :], acc[:, 2 * (b % 2) + t, :], ACT.Silu,
                                   scale=rstd[:, norm, t:t + 1]).then_inc(acc_freed[b % 2], 1)

            def turned_hi(j, dst, first, di=0):
                act.wait_ge(mt_turned, j + 2 + di)
                for t in range(TT):
                    act.activation(dst[:, bass.ds(first, 4), t * P:(t + 1) * P],
                                   tp[:, t, :].rearrange("p (a b) -> p a b", a=4), ACT.Copy).then_inc(mt_hi, 1)

            def out_squares(b, norm, j):
                act.wait_ge(chunk_done, chunks_through(b))
                for t in range(TT):
                    squares_before(norm, j, t)
                    act.activation(tmp[:, t, :], acc[:, 2 * (b % 2) + t, :], ACT.Square,
                                   accum_out=ssq[:, norm, t, j:j + 1]).then_inc(squares_ready, 1)

            def first_block(n, chunk, ahead):
                for c in range(DC):
                    normed_hi(n, c)
                    if c >= ahead:
                        split_hi(chunk + c)
                    if 4 <= c < 4 + TT * OUT_BLOCKS:
                        h_square(n, (c - 4) // TT, (c - 4) % TT)

            def split_ahead(chunk):
                for c in range(AHEAD):
                    split_hi(chunk + c)

            def ffn(c_in, c_out, b_in, b_out, m0, norm, n, ahead):
                first_block(n, c_in, ahead)
                with act.Fori(0, DFF // NB - 1) as i:
                    for c in range(DC):
                        split_hi(c_in + DC + c, i * (2 * DC))
                        if c == 8:
                            silu_gate(b_in, m0, norm, i)
                    for c in range(DC):
                        split_hi(c_in + 2 * DC + c, i * (2 * DC))
                        if c == 14:
                            turned_hi(m0, MH, i * 4, i)
                last = DFF // NB - 1
                for c in range(DC):
                    split_hi(c_out - DC + c)
                    if c == 8:
                        silu_gate(b_out - 2, m0 + last, norm)
                for b in range(OUT_BLOCKS):
                    for c in range(FC):
                        split_hi(c_out + b * FC + c)
                        if b == 0 and c == 14:
                            turned_hi(m0 + last, MH, 4 * last)
                        if b and c == 8:
                            out_squares(b_out + b - 1, norm + 1, b - 1)

            def copy_qt(q, first, k):
                act.wait_ge(qt_turned, q + 1)
                act.activation(QT[:, first:first + k, 0:P], tp[:, 2, 0:k * P].rearrange("p (a b) -> p a b", a=k),
                               ACT.Copy).then_inc(qt_act, 1)

            def exps(n, hd, a_head):
                act.wait_ge(nmax_ready, n + 1)
                if a_head:
                    act.activation(esink[:, n, :], nmax[:, n, :], ACT.Exp, bias=sink[:, hd:hd + 1]).then_inc(exp_ready, 1)
                for t in range(TT):
                    act.activation(prob[n % 2][:, t, :], prob[n % 2][:, t, :], ACT.Exp, bias=nmax[:, n, t:t + 1],
                                   accum_out=psum_[:, n, t:t + 1]).then_inc(exp_ready, 1)

            def copy_probT(n):
                act.wait_ge(prob_turned, n + 1)
                if n:
                    act.wait_ge(y_done, n)
                act.activation(probT[:, :, :], tp[:, 1, :].rearrange("p (a b) -> p a b", a=TT),
                               ACT.Copy).then_inc(probT_ready, 1)

            def split_y_hi(n, hd, a):
                act.wait_ge(y_done, n + 1)
                act.activation(YH[:, hd, a, :], tp[:, 2, 0:SEQ], ACT.Copy).then_inc(y_hi, 1)

            def finish_heads(c, g):
                if c == 2:
                    split_y_hi(2 * g, g, 1)
                    copy_probT(2 * g + 1)
                if c == 5:
                    split_y_hi(2 * g + 1, g, 0)

            def sigmoids(u):
                for side in range(2):
                    b = B_GATE + side * OUT_BLOCKS + u
                    act.wait_ge(acc_freed[b % 2], freed_before(b) + TT)
                    for t in range(TT):
                        g = gates[:, t, side * D + u * NB:side * D + (u + 1) * NB]
                        act.activation(g, g, ACT.Sigmoid).then_inc(sig_ready, 1)

            act.wait_ge(ident_ready, 2)
            act.activation(neghalf[:, :], ident[:, 0:TT], ACT.Copy, scale=0.0, bias=-0.5).then_inc(consts_ready, 1)
            act.wait_ge(mt_lo, 1)
            ffn(C_F1IN, C_F1OUT, B_F1IN, B_F1OUT, M_F1, 0, 0, 0)
            split_ahead(C_QKV)
            out_squares(B_QKV - 1, 1, 3)
            first_block(1, C_QKV, AHEAD)
            for b in range(1, QK_BLOCKS):
                for c in range(DC):
                    split_hi(C_QKV + b * DC + c)
                    if c == 12 and b - 1 < len(QK_HEADS):
                        copy_qt(b - 1, *QK_HEADS[b - 1])
            act.wait_ge(sink_landed, 16)
            for g in range(GATE_BLOCKS):
                for c in range(DC):
                    split_hi(C_GATE + g * DC + c)
                    if g:
                        finish_heads(c, g - 1)
                    if c == 9:
                        exps(2 * g, g, False)
                    if c == 11:
                        exps(2 * g + 1, g, True)
                    if c == 15:
                        copy_probT(2 * g)
            for u in range(OUT_BLOCKS):
                for c in range(16):
                    split_hi(C_UP + u * 16 + c)
                    if u == 0:
                        finish_heads(c, A_Q - 1)
                    if c == 10:
                        sigmoids(u)
                    if u and c == 14:
                        turned_hi(M_MIX + u - 1, XH, 4 * (u - 1))
            for b in range(OUT_BLOCKS):
                for c in range(DC):
                    split_hi(C_WOUT + b * DC + c)
                    if b and c == 8:
                        out_squares(B_WOUT + b - 1, 3, b - 1)
                    if b == 0 and c == 14:
                        turned_hi(M_MIX + 3, XH, 12)
            split_ahead(C_F2IN)
            out_squares(B_F2IN - 1, 3, 3)
            ffn(C_F2IN, C_F2OUT, B_F2IN, B_F2OUT, M_F2, 4, 2, AHEAD)
            out_squares(B_END - 1, 5, 3)

        @block.vector
        def _(dve):
            steps = [0]

            def done(ins):
                steps[0] += 1
                ins.then_inc(dve_step, 1)
                dve.wait_ge(dve_step, steps[0])

            def split_lo(c, more=0):
                dve.wait_ge(hi_ready, c + 1 + more)
                dve.tensor_tensor(WL[:, c % WS, :], raw[:, c // 2 % RAW, c % 2, :],
                                  WH[:, c % WS, :].bitcast(F32), ALU.subtract).then_inc(lo_ready, 1)

            def normed_lo(n, c):
                dve.wait_ge(xt_hi, DC * n + c + 1)
                dve.scalar_tensor_tensor(out=XL[:, c, :], in0=tp[:, c % 4, 0:SEQ],
                                         scalar=gainT[:, n * DC + c:n * DC + c + 1], in1=XH[:, c, :].bitcast(F32),
                                         op0=ALU.mult, op1=ALU.subtract).then_inc(xt_lo, 1)

            def mean_square(norm):
                done(dve.reduce_sum(ms[:, norm, :], ssq[:, norm, :, :], AX.X))
                dve.tensor_scalar(ms[:, norm, :], ms[:, norm, :], 1.0 / D, EPS, ALU.mult, ALU.add).then_inc(ms_ready, 1)

            def first_block(n, chunk, ahead):
                for c in range(DC):
                    if n and c == 0:
                        update_h(n - 1, 0)
                    if n and c % 4 == 0 and c < DC - 4:
                        update_h(n - 1, c // 4 + 1)
                    normed_lo(n, c)
                    if c >= ahead:
                        split_lo(chunk + c)
                dve.wait_ge(squares_ready, TT * OUT_BLOCKS * (2 * n + 1))
                mean_square(2 * n)

            def split_ahead(chunk):
                for c in range(AHEAD):
                    split_lo(chunk + c)

            def gate_times_up(b, norm, di=0):
                dve.wait_ge(chunk_done, chunks_through(b) + 2 * DC * di)
                dve.wait_ge(acc_freed[(b - 1) % 2], freed_before(b - 1) + TT + 2 * di)
                dve.wait_ge(rstd_ready, norm + 1)
                for t in range(TT):
                    dve.scalar_tensor_tensor(out=tmp[:, t, :], in0=acc[:, 2 * (b % 2) + t, :],
                                             scalar=rstd[:, norm, t:t + 1], in1=tmp[:, t, :],
                                             op0=ALU.mult, op1=ALU.mult).then_inc(acc_freed[b % 2], 1)

            def turned_lo(j, hi, lo, first, di=0):
                for t in range(TT):
                    dve.wait_ge(mt_hi, TT * j + t + 1 + TT * di)
                    dve.tensor_tensor(lo[:, bass.ds(first, 4), t * P:(t + 1) * P],
                                      tp[:, t, :].rearrange("p (a b) -> p a b", a=4),
                                      hi[:, bass.ds(first, 4), t * P:(t + 1) * P].bitcast(F32),
                                      ALU.subtract).then_inc(mt_lo, 1)

            def times_post_gain(b, n, j, gp, weight, tiles=range(TT)):
                dve.wait_ge(chunk_done, chunks_through(b))
                dve.wait_ge(post_gain_landed, 16 * (n + 1))
                for t in tiles:
                    dve.wait_ge(squares_ready, TT * OUT_BLOCKS * (2 * n + 1) + TT * j + t + 1)
                    dve.scalar_tensor_tensor(out=fg[:, t, j * NB:(j + 1) * NB], in0=acc[:, 2 * (b % 2) + t, :],
                                             scalar=weight, in1=gp[:, j * NB:(j + 1) * NB],
                                             op0=ALU.mult, op1=ALU.mult).then_inc(acc_freed[b % 2], 1)

            def post_norm(n, b_last, gp, weight):
                times_post_gain(b_last, n, OUT_BLOCKS - 1, gp, weight, (0,))
                dve.wait_ge(squares_ready, TT * OUT_BLOCKS * (2 * n + 2))
                mean_square(2 * n + 1)
                times_post_gain(b_last, n, OUT_BLOCKS - 1, gp, weight, (1,))
                for b in (b_last - 1, b_last):
                    dve.wait_ge(acc_freed[b % 2], freed_before(b) + TT)
                dve.wait_ge(rstd_ready, 2 * n + 2)

            def update_h(n, j):
                cols = slice(j * NB, (j + 1) * NB)
                for t in range(TT):
                    dve.scalar_tensor_tensor(out=h[:, t, cols], in0=fg[:, t, cols],
                                             scalar=rstd[:, 2 * n + 1, t:t + 1], in1=h[:, t, cols],
                                             op0=ALU.mult, op1=ALU.add).then_inc(h_ready, 1)

            def ffn(c_in, c_out, b_in, b_out, m0, norm, n, ahead):
                first_block(n, c_in, ahead)
                with dve.Fori(0, DFF // NB - 1) as i:
                    for c in range(DC):
                        split_lo(c_in + DC + c, i * (2 * DC))
                    for c in range(DC):
                        split_lo(c_in + 2 * DC + c, i * (2 * DC))
                        if c == 8:
                            gate_times_up(b_in + 1, norm, i)
                        if c == 14:
                            turned_lo(m0, MH, ML, i * 4, i)
                last = DFF // NB - 1
                for c in range(DC):
                    split_lo(c_out - DC + c)
                for b in range(OUT_BLOCKS):
                    for c in range(FC):
                        split_lo(c_out + b * FC + c)
                        if b == 0 and c == 8:
                            gate_times_up(b_out - 1, norm)
                        if b == 0 and c == 14:
                            turned_lo(m0 + last, MH, ML, 4 * last)
                        if b and c == 8:
                            times_post_gain(b_out + b - 1, n, b - 1, gp_ffn, 0.5)

            def read_qkv(q):
                b = B_QKV + q
                dve.wait_ge(chunk_done, chunks_through(b))
                if q == 0:
                    dve.wait_ge(rstd_ready, 3)
                else:
                    dve.wait_ge(qt_turned, min(q, len(QK_HEADS)))
                for t in range(TT):
                    a, r = acc[:, 2 * (b % 2) + t, :], rstd[:, 2, t:t + 1]
                    if q in (0, 1, 3, 4):
                        dve.tensor_scalar(tmp[:, t, :], a, r, SCALE, ALU.mult, ALU.mult).then_inc(acc_freed[b % 2], 1)
                    elif q in (5, 6):
                        dve.tensor_scalar(tmp[:, t, :], a, r, None, ALU.mult).then_inc(acc_freed[b % 2], 1)
                    elif q == 2:
                        half = A_KV * HD
                        dve.tensor_scalar(tmp[:, t, 0:half], a[:, 0:half], r, None, ALU.mult)
                        dve.tensor_scalar(V[:, t, 0:half], a[:, half:2 * half], r, None, ALU.mult).then_inc(acc_freed[b % 2], 1)
                    else:
                        v0 = A_KV * HD + (q - 7) * NB
                        dve.tensor_scalar(V[:, t, v0:v0 + NB], a, r, None, ALU.mult).then_inc(acc_freed[b % 2], 1)

            def copy_qt(q, first, k):
                dve.wait_ge(qt_turned, q + 1)
                dve.tensor_copy(QT[:, first:first + k, P:2 * P],
                                tp[:, 3, 0:k * P].rearrange("p (a b) -> p a b", a=k)).then_inc(qt_dve, 1)

            def read_gate(g):
                b = B_GATE + g
                dve.wait_ge(chunk_done, chunks_through(b))
                dve.wait_ge(gate_bias_landed, 16 * TT * (g + 1))
                for t in range(TT):
                    o = gates[:, t, g * NB:(g + 1) * NB]
                    dve.scalar_tensor_tensor(out=o, in0=acc[:, 2 * (b % 2) + t, :], scalar=rstd[:, 2, t:t + 1], in1=o,
                                             op0=ALU.mult, op1=ALU.add).then_inc(acc_freed[b % 2], 1)

            def logits(n, hd, a_head):
                dve.wait_ge(scores_done, n + 1)
                if n >= 2:
                    dve.wait_ge(prob_turned, n - 1)
                else:
                    dve.wait_ge(qt_turned, len(QK_HEADS))
                    dve.wait_ge(bias_ready, B_H)
                s = tp[:, 3 if a_head else 0, :].rearrange("p (t k) -> p t k", t=TT)
                if a_head:
                    dve.scalar_tensor_tensor(out=prob[n % 2][:, :, :], in0=distA[:, :, :], scalar=-SLOPES[hd], in1=s,
                                             op0=ALU.mult, op1=ALU.add).then_inc(logits_ready, 1)
                else:
                    dve.tensor_tensor(prob[n % 2][:, :, :], s, biasB[:, hd, :, :], ALU.add).then_inc(logits_ready, 1)
                dve.wait_ge(logits_ready, n + 1)
                done(dve.reduce_max(smax[:, n, :], prob[n % 2][:, :, :], AX.X))
                if a_head:
                    dve.tensor_scalar(nmax[:, n, :], smax[:, n, :], sink[:, hd:hd + 1], -1.0, ALU.max, ALU.mult).then_inc(nmax_ready, 1)
                else:
                    dve.tensor_scalar(nmax[:, n, :], smax[:, n, :], -1.0, None, ALU.mult).then_inc(nmax_ready, 1)

            def probabilities(n, hd, a_head):
                dve.wait_ge(exp_ready, 5 * hd + (5 if a_head else 2))
                if a_head:
                    done(dve.tensor_tensor(psum_[:, n, :], psum_[:, n, :], esink[:, n, :], ALU.add))
                done(dve.reciprocal(rinv[:, n, :], psum_[:, n, :]))
                for t in range(TT):
                    dve.tensor_scalar(prob[n % 2][:, t, :], prob[n % 2][:, t, :], rinv[:, n, t:t + 1], None, ALU.mult).then_inc(prob_ready, 1)

            def split_y_lo(n, hd, a):
                dve.wait_ge(y_hi, n + 1)
                dve.tensor_tensor(YL[:, hd, a, :], tp[:, 2, 0:SEQ], YH[:, hd, a, :].bitcast(F32),
                                  ALU.subtract).then_inc(y_lo, 1)

            def mix_a(u):
                b = B_UP + 2 * u
                dve.wait_ge(chunk_done, chunks_through(b))
                dve.wait_ge(sig_ready, 2 * TT * (u + 1))
                if u:
                    dve.wait_ge(mt_turned, M_MIX + u + 1)
                for t in range(TT):
                    dve.tensor_tensor(tmp[:, t, :], acc[:, 2 * (b % 2) + t, :], gates[:, t, u * NB:(u + 1) * NB],
                                      ALU.mult).then_inc(acc_freed[b % 2], 1)

            def mix_b(u):
                b = B_UP + 2 * u + 1
                dve.wait_ge(chunk_done, chunks_through(b))
                for t in range(TT):
                    g = gates[:, t, D + u * NB:D + (u + 1) * NB]
                    dve.tensor_tensor(g, acc[:, 2 * (b % 2) + t, :], g, ALU.mult).then_inc(acc_freed[b % 2], 1)
                for x in (b - 1, b):
                    dve.wait_ge(acc_freed[x % 2], freed_before(x) + TT)
                for t in range(TT):
                    g = gates[:, t, D + u * NB:D + (u + 1) * NB]
                    dve.tensor_tensor(tmp[:, t, :], tmp[:, t, :], g, ALU.add).then_inc(m_ready, 1)

            dve.wait_ge(mt_turned, 1)
            dve.tensor_copy(gainT[:, :], tp[:, 3, 0:3 * DC]).then_inc(mt_lo, 1)
            dve.wait_ge(mt_lo, 1)
            ffn(C_F1IN, C_F1OUT, B_F1IN, B_F1OUT, M_F1, 0, 0, 0)
            split_ahead(C_QKV)
            post_norm(0, B_QKV - 1, gp_ffn, 0.5)
            first_block(1, C_QKV, AHEAD)
            for b in range(1, QK_BLOCKS):
                for c in range(DC):
                    split_lo(C_QKV + b * DC + c)
                    if c == 8:
                        read_qkv(b - 1)
                    if c == 12 and b - 1 < len(QK_HEADS):
                        copy_qt(b - 1, *QK_HEADS[b - 1])
            dve.wait_ge(sink_landed, 16)
            dve.wait_ge(masks_landed, 32)
            for g in range(GATE_BLOCKS):
                for c in range(DC):
                    split_lo(C_GATE + g * DC + c)
                    if c == 2 and g:
                        split_y_lo(2 * g - 2, g - 1, 1)
                    if c == 5 and g:
                        split_y_lo(2 * g - 1, g - 1, 0)
                    if c == 8:
                        logits(2 * g, g, False)
                    if c == 9:
                        logits(2 * g + 1, g, True)
                    if c == 10 and g == 0:
                        read_qkv(QK_BLOCKS - 1)
                    if c == 11:
                        probabilities(2 * g, g, False)
                    if c == 12 and g:
                        read_gate(g - 1)
                    if c == 13:
                        probabilities(2 * g + 1, g, True)
            for u in range(OUT_BLOCKS):
                for c in range(16):
                    split_lo(C_UP + u * 16 + c)
                    if u == 0 and c == 2:
                        split_y_lo(14, 7, 1)
                    if u == 0 and c == 5:
                        split_y_lo(15, 7, 0)
                    if u == 0 and c == 8:
                        read_gate(GATE_BLOCKS - 1)
                    if u and c == 1:
                        mix_a(u - 1)
                    if u and c == 8:
                        mix_b(u - 1)
                    if u and c == 14:
                        turned_lo(M_MIX + u - 1, XH, XL, 4 * (u - 1))
            for b in range(OUT_BLOCKS):
                for c in range(DC):
                    split_lo(C_WOUT + b * DC + c)
                    if b == 0 and c == 1:
                        mix_a(OUT_BLOCKS - 1)
                    if b == 0 and c == 8:
                        mix_b(OUT_BLOCKS - 1)
                    if b == 0 and c == 14:
                        turned_lo(M_MIX + 3, XH, XL, 12)
                    if b and c == 8:
                        times_post_gain(B_WOUT + b - 1, 1, b - 1, gp_mix, 1.0)
            split_ahead(C_F2IN)
            post_norm(1, B_F2IN - 1, gp_mix, 1.0)
            ffn(C_F2IN, C_F2OUT, B_F2IN, B_F2OUT, M_F2, 4, 2, AHEAD)
            post_norm(2, B_END - 1, gp_ffn, 0.5)
            for j in range(OUT_BLOCKS):
                update_h(2, j)

        @block.tensor
        def _(pe):
            def chunk(c, b, hi, lo, first, last, more=0):
                pe.wait_ge(lo_ready, c + 1 + more)
                w = c % WS
                for t in range(TT):
                    a, tok = acc[:, 2 * (b % 2) + t, :], slice(t * P, (t + 1) * P)
                    pe.matmul(a, hi[:, tok], WH[:, w, :], start=first, stop=False)
                    pe.matmul(a, hi[:, tok], WL[:, w, :], start=False, stop=False)
                    mm = pe.matmul(a, lo[:, tok], WH[:, w, :], start=False, stop=last)
                mm.then_inc(chunk_done, 1)

            def acc_free(b, di=0):
                if freed_before(b):
                    pe.wait_ge(acc_freed[b % 2], freed_before(b) + 2 * di)

            def turn_h(n, c):
                if n:
                    pe.wait_ge(h_ready, TT * OUT_BLOCKS * (n - 1) + TT * (c // 4 + 1))
                else:
                    pe.wait_ge(x_landed[c // 4], 16)
                    if c == 3:
                        pe.wait_ge(mt_lo, 1)
                if c >= 4:
                    pe.wait_ge(xt_lo, DC * n + c - 3)
                for t in range(TT):
                    tr = pe.transpose(tp[:, c % 4, t * P:(t + 1) * P], h[:, t, c * P:(c + 1) * P], ident[:, :])
                tr.then_inc(xt_turned, 1)

            def first_block(n, c0, b):
                for c in range(4):
                    turn_h(n, c)
                acc_free(b)
                for c in range(DC):
                    pe.wait_ge(xt_lo, DC * n + c + 1)
                    chunk(c0 + c, b, XH[:, c, :], XL[:, c, :], c == 0, c == DC - 1)
                    if c + 4 < DC:
                        turn_h(n, c + 4)

            def turn_m(j, di=0):
                pe.wait_ge(mt_lo, 1 + TT * j + TT * di)
                for t in range(TT):
                    for a in range(4):
                        tr = pe.transpose(tp[:, t, a * P:(a + 1) * P], tmp[:, t, a * P:(a + 1) * P], ident[:, :])
                tr.then_inc(mt_turned, 1)

            def ffn(c_in, c_out, b_in, b_out, m0, n):
                first_block(n, c_in, b_in)
                acc_free(b_in + 1)
                with pe.Fori(0, DFF // NB - 1) as i:
                    b = b_in + 1
                    for c in range(DC):
                        chunk(c_in + DC + c, b, XH[:, c, :], XL[:, c, :], c == 0, c == DC - 1, i * (2 * DC))
                    b = b_in + 2
                    acc_free(b, i)
                    for c in range(DC):
                        if c == 5:
                            pe.wait_ge(acc_freed[(b - 1) % 2], freed_before(b - 1) + TT + 2 * i)
                            turn_m(m0, i)
                        chunk(c_in + 2 * DC + c, b, XH[:, c, :], XL[:, c, :], c == 0, c == DC - 1, i * (2 * DC))
                last = DFF // NB - 1
                b = b_out - 1
                acc_free(b)
                for c in range(DC):
                    chunk(c_out - DC + c, b, XH[:, c, :], XL[:, c, :], c == 0, c == DC - 1)
                for j in range(OUT_BLOCKS):
                    b = b_out + j
                    acc_free(b)
                    for c in range(FC):
                        if j == 0 and c == 0:
                            pe.wait_ge(mt_lo, 1 + TT * (m0 + last))
                        if j == 0 and c == 5:
                            pe.wait_ge(acc_freed[(b - 1) % 2], freed_before(b - 1) + TT)
                            turn_m(m0 + last)
                        if j == 0 and c == 4 * last:
                            pe.wait_ge(mt_lo, 1 + TT * (m0 + last + 1))
                        chunk(c_out + j * FC + c, b, MH[:, c, :], ML[:, c, :], c == 0, c == FC - 1)

            def turn_qk(q, k):
                b = B_QKV + q
                pe.wait_ge(acc_freed[b % 2], freed_before(b) + TT)
                if q:
                    pe.wait_ge(qt_act, q)
                    pe.wait_ge(qt_dve, q)
                for t in range(TT):
                    for a in range(k):
                        tr = pe.transpose(tp[:, 2 + t, a * P:(a + 1) * P], tmp[:, t, a * P:(a + 1) * P], ident[:, :])
                tr.then_inc(qt_turned, 1)

            def scores(n, qi, ki, bank):
                if n == 0:
                    pe.wait_ge(qt_act, len(QK_HEADS))
                    pe.wait_ge(qt_dve, len(QK_HEADS))
                if n >= 2:
                    pe.wait_ge(logits_ready, n - 1)
                for t in range(TT):
                    mm = pe.matmul(tp[:, bank, t * SEQ:(t + 1) * SEQ], QT[:, qi, t * P:(t + 1) * P], QT[:, ki, :],
                                   start=True, stop=True)
                mm.then_inc(scores_done, 1)

            def turn_prob(n):
                pe.wait_ge(prob_ready, TT * (n + 1))
                if n:
                    pe.wait_ge(probT_ready, n)
                for kt in range(TT):
                    for t in range(TT):
                        o = kt * SEQ + t * P
                        tr = pe.transpose(tp[:, 1, o:o + P], prob[n % 2][:, t, kt * P:(kt + 1) * P], ident[:, :])
                tr.then_inc(prob_turned, 1)

            def weighted_values(n, v0):
                if n == 0:
                    for b in (B_GATE - 2, B_GATE - 1):
                        pe.wait_ge(acc_freed[b % 2], freed_before(b) + TT)
                pe.wait_ge(probT_ready, n + 1)
                if n:
                    pe.wait_ge(y_lo, n)
                for kt in range(TT):
                    mm = pe.matmul(tp[:, 2, 0:SEQ], V[:, kt, v0:v0 + HD], probT[:, kt, :], start=kt == 0, stop=kt == TT - 1)
                mm.then_inc(y_done, 1)

            pe.wait_ge(ident_ready, 2)
            pe.wait_ge(gain_landed, 48)
            pe.transpose(tp[:, 3, 0:3 * DC], grows[:, :], ident[0:3 * DC, 0:3 * DC]).then_inc(mt_turned, 1)
            ffn(C_F1IN, C_F1OUT, B_F1IN, B_F1OUT, M_F1, 0)
            first_block(1, C_QKV, B_QKV)
            for j in range(1, QK_BLOCKS):
                acc_free(B_QKV + j)
                for c in range(DC):
                    if c == 3 and j - 1 < len(QK_HEADS):
                        turn_qk(j - 1, QK_HEADS[j - 1][1])
                    chunk(C_QKV + j * DC + c, B_QKV + j, XH[:, c, :], XL[:, c, :], c == 0, c == DC - 1)
            for g in range(GATE_BLOCKS):
                acc_free(B_GATE + g)
                for c in range(DC):
                    if c == 0:
                        scores(2 * g, 10 + g, 18 + g, 0)
                        scores(2 * g + 1, g, 8 + g // 4, 3)
                    if c == 7:
                        turn_prob(2 * g)
                    if c == 9:
                        turn_prob(2 * g + 1)
                    if c == 10:
                        weighted_values(2 * g, (A_KV + g) * HD)
                    if c == 13:
                        weighted_values(2 * g + 1, g // 4 * HD)
                    chunk(C_GATE + g * DC + c, B_GATE + g, XH[:, c, :], XL[:, c, :], c == 0, c == DC - 1)
            for u in range(OUT_BLOCKS):
                for side in range(2):
                    b = B_UP + 2 * u + side
                    acc_free(b)
                    for c in range(8):
                        if u == 0 and side == 0 and c == 0:
                            pe.wait_ge(y_lo, 15)
                        if u == 0 and side == 0 and c == 7:
                            pe.wait_ge(y_lo, 16)
                        if u and side == 0 and c == 5:
                            pe.wait_ge(m_ready, TT * u)
                            turn_m(M_MIX + u - 1)
                        chunk(C_UP + u * 16 + side * 8 + c, b, YH[:, c, side, :], YL[:, c, side, :], c == 0, c == 7)
            for j in range(OUT_BLOCKS):
                b = B_WOUT + j
                acc_free(b)
                for c in range(DC):
                    if j == 0 and c == 0:
                        pe.wait_ge(mt_lo, 1 + TT * (M_MIX + 3))
                    if j == 0 and c == 5:
                        pe.wait_ge(m_ready, TT * OUT_BLOCKS)
                        turn_m(M_MIX + 3)
                    if j == 0 and c == 12:
                        pe.wait_ge(mt_lo, 1 + TT * (M_MIX + 4))
                    chunk(C_WOUT + j * DC + c, b, XH[:, c, :], XL[:, c, :], c == 0, c == DC - 1)
            ffn(C_F2IN, C_F2OUT, B_F2IN, B_F2OUT, M_F2, 2)


INPUTS = ["x", "ffn1_pre_g", "ffn1_w_in", "ffn1_w_out", "ffn1_post_g", "mix_pre_g", "w_in", "b_gate", "sink_a",
          "rpb_b", "w_up_a", "w_up_b", "w_out", "mix_post_g", "ffn2_pre_g", "ffn2_w_in", "ffn2_w_out", "ffn2_post_g"]


def window_constants():
    t = np.arange(SEQ)
    dist = np.abs(t[:, None] - t[None, :]).astype(np.float32)
    dist[dist > 128] = 1e33
    col = t % GRID_W
    start = np.clip(col - 8, 0, GRID_W - 16)
    inside = (col[None, :] >= start[:, None]) & (col[None, :] < start[:, None] + 16)
    return dist, np.where(inside, 0.0, -1e30).astype(np.float32)


def kernel(**inputs):
    from concourse import bacc
    from concourse.bass_utils import run_bass_kernel_spmd

    nc = bacc.Bacc("TRN2", target_bir_lowering=False, num_devices=1)
    arrays = {f"in_{n}": np.ascontiguousarray(inputs[n]) for n in INPUTS}
    arrays["in_alibi_dist"], arrays["in_natten_mask"] = window_constants()
    args = [nc.dram_tensor(n, a.shape, mybir.dt.from_np(a.dtype), kind="ExternalInput").ap() for n, a in arrays.items()]
    out = nc.dram_tensor("out_h", (1, SEQ, D), F32, kind="ExternalOutput").ap()
    layer_kernel(nc, *args, out)
    result = run_bass_kernel_spmd(nc, [arrays], core_ids=[0])
    return result.results[0]["out_h"]
```
